# Optimizing a Trainium2 kernel written in Bass

```python
import jax, jax.numpy as jnp
from jax import lax
import numpy as np

D_MODEL = 2048
BATCH = 1
SEQ = 512
DEPTH = 2

CHUNK = 64
N_MEM = 256
N_A_LAYERS = DEPTH // 2
N_B_LAYERS = DEPTH - N_A_LAYERS
D_RNN = 3 * D_MODEL // 4
RNN_BLOCK = 128
N_RNN_BLOCKS = D_RNN // RNN_BLOCK
CONV_WIDTH = 4
LRU_C = 8.0
SB_HEAD_DIM = 128
D_SB = 3 * D_MODEL // 4
N_SB_HEADS = D_SB // SB_HEAD_DIM
N_MEM_HEADS = 4
MEM_HEAD_DIM = 128
D_MEM = N_MEM_HEADS * MEM_HEAD_DIM
D_MIX = D_RNN + D_MEM
Q_BLOCK = 128
EPS = 1e-6

kernel_name = "yoco_rglru_stickbreaking_memory_trunk"

def rms_norm(x, g):
    xf = x.astype(jnp.float32)
    y = xf * lax.rsqrt(jnp.mean(xf * xf, axis=-1, keepdims=True) + EPS)
    return (y * g.astype(jnp.float32)).astype(x.dtype)

def memory_attention(q, mem_k, mem_v):
    b, t, _ = q.shape
    qh = q.reshape(b, t, N_MEM_HEADS, MEM_HEAD_DIM)
    kh = mem_k.reshape(b, N_MEM, N_MEM_HEADS, MEM_HEAD_DIM)
    vh = mem_v.reshape(b, N_MEM, N_MEM_HEADS, MEM_HEAD_DIM)
    s = jnp.einsum('bthd,bmhd->bhtm', qh, kh).astype(jnp.float32) * (MEM_HEAD_DIM ** -0.5)
    p = jax.nn.softmax(s, axis=-1).astype(vh.dtype)
    o = jnp.einsum('bhtm,bmhd->bthd', p, vh)
    return o.reshape(b, t, D_MEM)

def causal_depthwise_conv(x, w, bias):
    y = lax.conv_general_dilated(
        x, w[:, None, :], window_strides=(1,), padding=[(CONV_WIDTH - 1, 0)],
        dimension_numbers=('NWC', 'WIO', 'NWC'), feature_group_count=x.shape[-1])
    return y + bias

def rg_lru(x, w_r, b_r, w_i, b_i, lam):
    b, t, _ = x.shape
    xb = x.reshape(b, t, N_RNN_BLOCKS, RNN_BLOCK)
    r = jax.nn.sigmoid(jnp.einsum('btnc,ncd->btnd', xb, w_r).reshape(b, t, D_RNN) + b_r)
    i = jax.nn.sigmoid(jnp.einsum('btnc,ncd->btnd', xb, w_i).reshape(b, t, D_RNN) + b_i)
    log_a = (-LRU_C * jax.nn.softplus(-lam.astype(jnp.float32))) * r.astype(jnp.float32)
    a = jnp.exp(log_a)
    u = jnp.sqrt(-jnp.expm1(2.0 * log_a)) * (i * x).astype(jnp.float32)

    def combine(left, right):
        a1, h1 = left
        a2, h2 = right
        return a1 * a2, a2 * h1 + h2

    _, h = lax.associative_scan(combine, (a, u), axis=1)
    return h.astype(x.dtype)

def stick_breaking_attention(q, k, v):
    b, t, _ = q.shape
    n_blk = t // Q_BLOCK
    qh = q.reshape(b, n_blk, Q_BLOCK, N_SB_HEADS, SB_HEAD_DIM).transpose(1, 0, 3, 2, 4)
    kh = k.reshape(b, t, N_SB_HEADS, SB_HEAD_DIM).transpose(0, 2, 1, 3)
    vh = v.reshape(b, t, N_SB_HEADS, SB_HEAD_DIM).transpose(0, 2, 1, 3)
    key_pos = jnp.arange(t)
    scale = SB_HEAD_DIM ** -0.5

    def one_block(args):
        q_blk, blk = args
        q_pos = blk * Q_BLOCK + jnp.arange(Q_BLOCK)
        mask = key_pos[None, :] < q_pos[:, None]
        z = jnp.einsum('bhqd,bhkd->bhqk', q_blk, kh).astype(jnp.float32) * scale
        log_beta = jax.nn.log_sigmoid(z)
        log_keep = jnp.where(mask, jax.nn.log_sigmoid(-z), 0.0)
        later = lax.cumsum(log_keep, axis=3, reverse=True) - log_keep
        w = jnp.where(mask, jnp.exp(log_beta + later), 0.0)
        return jnp.einsum('bhqk,bhkd->bhqd', w.astype(vh.dtype), vh)

    o = lax.map(one_block, (qh, jnp.arange(n_blk)))
    return o.transpose(1, 0, 3, 2, 4).reshape(b, t, D_SB)

def layer_a(h, g_norm, w_in, conv_w, conv_b, w_r, b_r, w_i, b_i, lam, w_out, mem_k, mem_v):
    u = rms_norm(h, g_norm)
    proj = u @ w_in
    x_rnn, g_rnn, q_mem, g_mem = jnp.split(proj, [D_RNN, 2 * D_RNN, 2 * D_RNN + D_MEM], axis=-1)
    x_rnn = causal_depthwise_conv(x_rnn, conv_w, conv_b)
    y_rnn = rg_lru(x_rnn, w_r, b_r, w_i, b_i, lam) * jax.nn.silu(g_rnn)
    y_mem = memory_attention(q_mem, mem_k, mem_v) * jax.nn.silu(g_mem)
    return h + jnp.concatenate([y_rnn, y_mem], axis=-1) @ w_out

def layer_b(h, g_norm, w_in, w_out, k_sb, v_sb, mem_k, mem_v):
    u = rms_norm(h, g_norm)
    proj = u @ w_in
    q_sb, g_sb, q_mem, g_mem = jnp.split(proj, [D_SB, 2 * D_SB, 2 * D_SB + D_MEM], axis=-1)
    y_sb = stick_breaking_attention(q_sb, k_sb, v_sb) * jax.nn.silu(g_sb)
    y_mem = memory_attention(q_mem, mem_k, mem_v) * jax.nn.silu(g_mem)
    return h + jnp.concatenate([y_sb, y_mem], axis=-1) @ w_out

def setup_inputs(seed: int = 0) -> dict:
    key = jax.random.key(seed)
    ks = jax.random.split(key, 24)
    f32 = jnp.float32

    def normal(k, shape, scale):
        return jax.random.normal(k, shape, f32) * scale

    def gain(k, shape):
        return 1.0 + 0.02 * jax.random.normal(k, shape, f32)

    a_pow = jax.random.uniform(ks[13], (N_A_LAYERS, D_RNN), f32, 0.9, 0.999)
    s = a_pow ** (1.0 / LRU_C)
    lru_lambda = jnp.log(s) - jnp.log1p(-s)
    return {
        "x": normal(ks[0], (BATCH, SEQ, D_MODEL), 1.0),
        "mem": normal(ks[1], (BATCH, N_MEM, D_MODEL), 1.0),
        "mem_norm": gain(ks[2], (D_MODEL,)),
        "w_mem_kv": normal(ks[3], (DEPTH, D_MODEL, 2 * D_MEM), D_MODEL ** -0.5),
        "norm_a": gain(ks[4], (N_A_LAYERS, D_MODEL)),
        "w_in_a": normal(ks[5], (N_A_LAYERS, D_MODEL, 2 * D_RNN + 2 * D_MEM), D_MODEL ** -0.5),
        "conv_w": normal(ks[6], (N_A_LAYERS, CONV_WIDTH, D_RNN), CONV_WIDTH ** -0.5),
        "conv_b": normal(ks[7], (N_A_LAYERS, D_RNN), 0.01),
        "w_rec_gate": normal(ks[8], (N_A_LAYERS, N_RNN_BLOCKS, RNN_BLOCK, RNN_BLOCK), RNN_BLOCK ** -0.5),
        "b_rec_gate": normal(ks[9], (N_A_LAYERS, D_RNN), 0.01),
        "w_in_gate": normal(ks[10], (N_A_LAYERS, N_RNN_BLOCKS, RNN_BLOCK, RNN_BLOCK), RNN_BLOCK ** -0.5),
        "b_in_gate": normal(ks[11], (N_A_LAYERS, D_RNN), 0.01),
        "lru_lambda": lru_lambda,
        "w_out_a": normal(ks[12], (N_A_LAYERS, D_MIX, D_MODEL), D_MIX ** -0.5),
        "kv_norm": gain(ks[14], (D_MODEL,)),
        "w_kv": normal(ks[15], (D_MODEL, 2 * D_SB), D_MODEL ** -0.5),
        "norm_b": gain(ks[16], (N_B_LAYERS, D_MODEL)),
        "w_in_b": normal(ks[17], (N_B_LAYERS, D_MODEL, 2 * D_SB + 2 * D_MEM), D_MODEL ** -0.5),
        "w_out_b": normal(ks[18], (N_B_LAYERS, D_SB + D_MEM, D_MODEL), (D_SB + D_MEM) ** -0.5),
        "final_norm": gain(ks[19], (D_MODEL,)),
    }

def reference(x, mem, mem_norm, w_mem_kv, norm_a, w_in_a, conv_w, conv_b, w_rec_gate, b_rec_gate,
              w_in_gate, b_in_gate, lru_lambda, w_out_a, kv_norm, w_kv, norm_b, w_in_b, w_out_b,
              final_norm):
    mem_n = rms_norm(mem, mem_norm)
    h = x
    k_sb = None
    v_sb = None
    for layer in range(DEPTH):
        mem_k, mem_v = jnp.split(mem_n @ w_mem_kv[layer], 2, axis=-1)
        if layer < N_A_LAYERS:
            h = layer_a(h, norm_a[layer], w_in_a[layer], conv_w[layer], conv_b[layer],
                        w_rec_gate[layer], b_rec_gate[layer], w_in_gate[layer], b_in_gate[layer],
                        lru_lambda[layer], w_out_a[layer], mem_k, mem_v)
            if layer == N_A_LAYERS - 1:
                k_sb, v_sb = jnp.split(rms_norm(h, kv_norm) @ w_kv, 2, axis=-1)
        else:
            j = layer - N_A_LAYERS
            h = layer_b(h, norm_b[j], w_in_b[j], w_out_b[j], k_sb, v_sb, mem_k, mem_v)
    return rms_norm(h, final_norm)


_drawn_inputs = setup_inputs


def setup_inputs(seed=0):
    import zlib

    import numpy as np

    out = dict(_drawn_inputs(seed))
    spreads = {}
    factors = {'mem_norm': 8.0,
     'norm_a': 6.601,
     'b_rec_gate': 8.0,
     'b_in_gate': 8.0,
     'kv_norm': 8.0,
     'norm_b': 8.0,
     'final_norm': 2.916}
    for name, (base, spread) in spreads.items():
        noise = np.random.default_rng([zlib.crc32(name.encode()), seed]).standard_normal(out[name].shape)
        drawn = base * np.exp(spread * noise) if base else spread * noise
        out[name] = __import__('jax').numpy.asarray(drawn.astype(out[name].dtype))
    for name, factor in factors.items():
        out[name] = (out[name] * factor).astype(out[name].dtype)
    return out
```

```python
from contextlib import ExitStack

import concourse.bass as bass
from concourse import mybir

P = 128
T = 512
D = 2048
NK = D // P
KS = 4
C = 512
NT = T // P
M = 256
NMB = M // P
DR = 3 * D // 4
NB = DR // P
NPAIR = NB // 4
MH = 4
EPS = 1e-6
LRU_C = 8.0
SCALE = float(P) ** -0.5
CONV = 4

G_MEM = 0
G_A = 4
G_OUTA = 12
G_KV = 16
G_B = 22
G_OUTB = 30
F_MEM, F_X, F_YA, F_H, F_YB = 0, 4, 8, 12, 16

Z_ORDER = ((1, 3, 0), (0, 2, 384), (2, 2, 0), (3, 1, 0))

F32 = mybir.dt.float32
F32R = mybir.dt.float32r
ALU = mybir.AluOpType
ACT = mybir.ActivationFunctionType
AX_X = mybir.AxisListType.X


def in_column(q):
    return (q // 2) * C + (q % 2) * DR if q < 2 * NPAIR else 2 * DR + (q - 2 * NPAIR) * C


def transposed_before(f):
    return f if f < F_YA else f - 4


class Chain:

    def __init__(self, eng, sem):
        self.eng, self.sem, self.base, self.n = eng, sem, 0, 0

    def mark(self, ins):
        ins.then_inc(self.sem, 1)
        self.n += 1
        return self.base + self.n

    def wait(self, value):
        self.eng.wait_ge(self.sem, value)

    def link(self, ins):
        self.wait(self.mark(ins))

    def enter(self, i, per):
        self.total = self.base + self.n
        self.base, self.n, self.per = self.total + i * per, 0, per

    def leave(self, turns):
        assert self.n == self.per, self.n
        self.base, self.n = self.total + turns * self.per, 0


def trunk(nc, x, mem, mem_norm, w_mem_kv, norm_a, w_in_a, conv_w, conv_b, w_rec_gate, b_rec_gate,
          w_in_gate, b_in_gate, lru_lambda, w_out_a, kv_norm, w_kv, norm_b, w_in_b, w_out_b,
          final_norm, out):
    x_v = x.rearrange("b (t p) n -> (b p) t n", p=P)
    mem_v = mem.rearrange("b (t p) n -> (b p) t n", p=P)
    out_v = out.rearrange("b (t p) n -> (b p) t n", p=P)
    wa, woa, wb, wob = w_in_a[0], w_out_a[0], w_in_b[0], w_out_b[0]
    y_dram = nc.dram_tensor("y_scratch", [NK, P, T], F32, kind="Internal").ap()
    y2_dram = nc.dram_tensor("y2_scratch", [NK, P, T], F32, kind="Internal").ap()
    h_dram = nc.dram_tensor("h_scratch", [T, D], F32, kind="Internal").ap()
    h_v = h_dram.rearrange("(t p) n -> p t n", p=P)
    k_dram = nc.dram_tensor("k_scratch", [NB, P, T], F32, kind="Internal").ap()
    v_dram = nc.dram_tensor("v_scratch", [T, DR], F32, kind="Internal").ap()
    v_v = v_dram.rearrange("(t p) n -> p t n", p=P)

    with ExitStack() as ctx:
        def sb(name, shape, dt=F32):
            return ctx.enter_context(nc.sbuf_tensor(name, shape, dt))

        def sem(name):
            return ctx.enter_context(nc.semaphore(name))

        act_hi = sb("act_hi", [P, NK, T], F32R)
        act_lo = sb("act_lo", [P, NK, T], F32R)
        w_hi = sb("w_hi", [P, 2, KS, C], F32R)
        w_lo = sb("w_lo", [P, 2, KS, C], F32R)
        w_raw = sb("w_raw", [P, 2, KS, C])
        f_raw = sb("f_raw", [P, 2, 4, C])
        memt_hi = act_hi[:, 8:16, :].rearrange("p a (b m) -> p (a b) m", m=M)
        memt_lo = act_lo[:, 8:16, :].rearrange("p a (b m) -> p (a b) m", m=M)
        km = sb("km", [P, 2, MH, M])
        vm = sb("vm", [P, 2, NMB, MH * P])
        work = sb("work", [P, 2060 + 8 * 2048])
        xr = work[:, 0:2060].rearrange("p (b t) -> p b t", b=4)

        def block(n):
            return work[:, 2060 + 2048 * n:2060 + 2048 * (n + 1)]

        def four(n):
            return block(n).rearrange("p (b t) -> p b t", b=4)

        xc, ra, ig, th, gg, sg = four(0), four(1), four(2), four(3), four(4), four(5)
        keep, beta, ot = xc, ra, th
        wt = block(2)[:, 0:1280]
        gate_w = block(6)[:, 0:1024].rearrange("p (g b c) -> p g b c", g=2, b=4)
        kbuf = block(6)[:, 0:1024].rearrange("p (r t) -> p r t", r=2)
        vbuf = block(6)[:, 1024:2048].rearrange("p (r t d) -> p r t d", r=2, t=NT)
        pm = block(0)[:, 0:1024].rearrange("p (t m) -> p t m", t=NT)
        pmt = block(0)[:, 1024:2048].rearrange("p (m t) -> p m t", m=NMB)
        stage = four(7)
        junk = four(0)
        h2 = work[:, 2060:2060 + 4 * 2048].rearrange("p (t c n) -> p t c n", t=NT, c=4)
        fgain = block(4)
        ident = sb("ident", [P, P])
        ones = sb("ones", [P, P])
        m_keep = sb("m_keep", [P, P])
        m_beta = sb("m_beta", [P, P])
        rstd_bc = sb("rstd_bc", [P, T])
        gains = sb("gains", [P, 64])
        chan = sb("chan", [P, 96])
        vec_raw = block(6)[:, 0:256].rearrange("p (a n) -> p a n", a=2)
        diag = four(7)
        g_mem, g_a, g_kv, g_b = (gains[:, 16 * n:16 * n + 16] for n in range(4))
        c_neg = sb("c_neg", [P, NB])
        c_pos = sb("c_pos", [P, NB])
        lt = sb("lt", [P, 4, NB])
        ss = sb("ss", [P, 4, 4])
        ms = sb("ms", [P, 4])
        rms = sb("rms", [P, 4])
        rstd = sb("rstd", [P, 4])
        rstd_m = sb("rstd_m", [P, 4])
        mx = sb("mx", [P, 4])
        nmx = sb("nmx", [P, 4])
        rsum = sb("rsum", [P, 4])
        rinv = sb("rinv", [P, 4])

        main = ctx.enter_context(nc.psum_tensor("main", [P, 4, C], F32))
        aux = ctx.enter_context(nc.psum_tensor("aux", [P, 4, C], F32))

        w_loaded = [sem("w_loaded0"), sem("w_loaded1")]
        f_loaded = [sem("f_loaded0"), sem("f_loaded1")]
        vec_loaded = sem("vec_loaded")
        chan_loaded = sem("chan_loaded")
        hi_ready = sem("hi_ready")
        lo_ready = sem("lo_ready")
        slab_done = sem("slab_done")
        bank_done = sem("bank_done")
        bank_free = sem("bank_free")
        fill_tr = sem("fill_tr")
        fill_hi = sem("fill_hi")
        fill_lo = sem("fill_lo")
        const_ready = sem("const_ready")
        const_step = sem("const_step")
        vec_t = sem("vec_t")
        vec_copied = sem("vec_copied")
        lam_exp = sem("lam_exp")
        lam_in = sem("lam_in")
        lam_ready = sem("lam_ready")
        ms_ready = sem("ms_ready")
        rms_ready = sem("rms_ready")
        diag_ready = sem("diag_ready")
        bc_done = sem("bc_done")
        km_ready = sem("km_ready")
        kmt_done = sem("kmt_done")
        kmt_read = sem("kmt_read")
        gate_loaded = sem("gate_loaded")
        xc_ready = sem("xc_ready")
        gates_done = sem("gates_done")
        gates_read = sem("gates_read")
        decay_ready = sem("decay_ready")
        v_ready = sem("v_ready")
        root_ready = sem("root_ready")
        sg_ready = sem("sg_ready")
        y_ready = sem("y_ready")
        y_stored = sem("y_stored")
        resid_loaded = sem("resid_loaded")
        h_stored = sem("h_stored")
        kv_stored = sem("kv_stored")
        kv_loaded = [sem("kv_loaded0"), sem("kv_loaded1")]
        z_done = sem("z_done")
        z_read = sem("z_read")
        w_ready = sem("w_ready")
        wt_done = sem("wt_done")
        wt_read = sem("wt_read")
        o_done = sem("o_done")
        ms_done = sem("ms_done")
        nmx_ready = sem("nmx_ready")
        p_exp = sem("p_exp")
        p_ready = sem("p_ready")
        pt_done = sem("pt_done")
        pt_read = sem("pt_read")
        mo_done = sem("mo_done")
        mo_read = sem("mo_read")
        h2_loaded = sem("h2_loaded")
        sq_ready = sem("sq_ready")
        scaled = sem("scaled")
        last_gain = sem("last_gain")
        pregain = sem("pregain")
        out_stored = sem("out_stored")
        dve_chain = sem("dve_chain")
        act_chain = sem("act_chain")

        blk = ctx.enter_context(nc.Block())

        @blk.sync
        def _(sp):
            def load_slab(G, j, src, rows=None):
                if not (isinstance(G, int) and 4 * G + j < 2):
                    sp.wait_ge(lo_ready, 4 * (4 * G + j - 1))
                sp.dma_start(w_raw[:, j % 2, :, :],
                             src[C * j:C * (j + 1), :].rearrange("(k p) n -> p k n", p=P)
                             ).then_inc(w_loaded[j % 2], 16)

            def load_fill(f, src, width=4):
                if f >= 2:
                    sp.wait_ge(fill_lo, 4 * (f - 1))
                sp.dma_start(f_raw[:, f % 2, 0:width, :], src).then_inc(f_loaded[f % 2], 16)

            def load_in(w, G0):
                def group(G, col):
                    for j in range(4):
                        load_slab(G, j, w[:, bass.ds(col, C)])
                for j in range(4):
                    load_slab(G0, j, w[:, 0:C])
                    if G0 == G_A and j == 0:
                        load_fill(F_X + 3, x_v[:, :, 3 * C:4 * C])
                with sp.Fori(0, NPAIR - 1) as i:
                    group(2 * i + (G0 + 1), C * i + DR)
                    group(2 * i + (G0 + 2), C * i + C)
                for q in range(2 * NPAIR - 1, 2 * NPAIR + 2):
                    group(G0 + q, in_column(q))

            for n, (v, k) in enumerate(((mem_norm, 1), (norm_a[0], 1), (kv_norm, 1), (norm_b[0], 1))):
                sp.dma_start(vec_raw[16 * n:16 * n + 16, 0, :], v.rearrange("(a p) -> a p", p=P)
                             ).then_inc(vec_loaded, 16)
            for m in range(4):
                for j in range(4):
                    if m == 0:
                        load_fill(F_MEM + j, mem_v[:, :, C * j:C * j + C], NMB)
                    load_slab(m, j, w_mem_kv[m // 2, :, C * (m % 2):C * (m % 2) + C])
                    if m == 0 and j == 1:
                        sp.dma_start(vec_raw[0:48, 1, :], conv_w[0].rearrange("j (c p) -> (j c) p", p=P)
                                     ).then_inc(chan_loaded, 16)
                        for n, v in enumerate((conv_b, b_rec_gate, b_in_gate, lru_lambda)):
                            sp.dma_start(vec_raw[48 + 12 * n:60 + 12 * n, 1, :], v[0].rearrange("(c p) -> c p", p=P)
                                         ).then_inc(chan_loaded, 16)
                    if m >= 1 and j == 0:
                        load_fill(F_X + m - 1, x_v[:, :, C * (m - 1):C * m])
            load_in(wa, G_A)

            def load_out(w, G0, y, f0, ystart):
                for j in range(4):
                    sp.wait_ge(y_stored, ystart + 16 * (j + 1))
                    load_fill(f0 + j, y[4 * j:4 * j + 4].rearrange("k p t -> p k t"))
                    load_slab(G0, j, w[:, 0:C])

            load_out(woa, G_OUTA, y_dram, F_YA, 0)
            with sp.Fori(0, 3) as i:
                for j in range(4):
                    load_slab(i + (G_OUTA + 1), j, woa[:, bass.ds(C * i + C, C)])
            for j in range(4):
                sp.wait_ge(h_stored, 16 * (j + 1))
                load_fill(F_H + j, h_v[:, :, C * j:C * j + C])
                load_slab(G_KV, j, w_kv[:, 0:C])
            with sp.Fori(0, 5) as i:
                for j in range(4):
                    load_slab(i + (G_KV + 1), j, w_kv[:, bass.ds(C * i + C, C)])
            load_in(wb, G_B)
            load_out(wob, G_OUTB, y2_dram, F_YB, 64)
            with sp.Fori(0, 3) as i:
                for j in range(4):
                    load_slab(i + (G_OUTB + 1), j, wob[:, bass.ds(C * i + C, C)])
            for t in range(NT):
                for half in range(2):
                    sp.wait_ge(scaled, 2 * t + half + 1)
                    sp.dma_start(out_v[:, t, 1024 * half:1024 * half + 1024],
                                 h2[:, t, 2 * half:2 * half + 2].rearrange("p c n -> p (c n)")).then_inc(out_stored, 16)
            sp.wait_ge(out_stored, 16 * 2 * NT)

        @blk.gpsimd
        def _(pool):
            nc.gpsimd.memset(ident[:], 0.0).then_inc(const_step, 1)
            nc.gpsimd.memset(m_keep[:], 1.0).then_inc(const_step, 1)
            nc.gpsimd.memset(m_beta[:], 1.0).then_inc(const_step, 1)
            nc.gpsimd.memset(ones[:], 1.0).then_inc(const_step, 1)
            nc.gpsimd.memset(xr[:, :, 0:3], 0.0).then_inc(const_step, 1)
            pool.wait_ge(const_step, 5)
            nc.gpsimd.affine_select(out=ident[:], in_=ident[:], compare_op=ALU.not_equal, fill=1.0, base=0,
                                    pattern=[[-1, P]], channel_multiplier=1).then_inc(const_ready, 1)
            nc.gpsimd.affine_select(out=m_keep[:], in_=m_keep[:], compare_op=ALU.is_ge, fill=0.0, base=0,
                                    pattern=[[1, P]], channel_multiplier=-1).then_inc(const_ready, 1)
            nc.gpsimd.affine_select(out=m_beta[:], in_=m_beta[:], compare_op=ALU.is_gt, fill=0.0, base=0,
                                    pattern=[[-1, P]], channel_multiplier=1).then_inc(const_ready, 1)
            for t in range(NT):
                pool.wait_ge(sq_ready, 12 + t + 1)
                nc.gpsimd.tensor_tensor(h2[:, t, 3, :], h2[:, t, 3, :], fgain[:, 3 * C:4 * C], ALU.mult
                                        ).then_inc(last_gain, 1)

        @blk.scalar
        def _(act):
            def split(G, j, gain=None):
                if not (isinstance(G, int) and 4 * G + j < 2):
                    act.wait_ge(slab_done, 4 * G + j - 1)
                act.wait_ge(w_loaded[j % 2], 16 * (2 * G + j // 2 + 1))
                for k in range(KS):
                    s = 1.0 if gain is None else gain[:, KS * j + k:KS * j + k + 1]
                    nc.scalar.activation(w_hi[:, j % 2, k, :], w_raw[:, j % 2, k, :], ACT.Copy, scale=s
                                         ).then_inc(hi_ready, 1)

            def split_next(G, j, gain, next_gain=None):
                if j < 3:
                    split(G, j + 1, gain)
                else:
                    split(G + 1, 0, next_gain)

            def fill(f, c, dst, nt, freed=None):
                act.wait_ge(f_loaded[f % 2], 16 * (f // 2 + 1))
                if f:
                    act.wait_ge(fill_hi, 4 * f)
                for t in range(nt):
                    nc.scalar.activation(junk[:, t, :], f_raw[:, f % 2, t, :], ACT.Square, accum_out=ss[:, t, c:c + 1])
                if freed is not None:
                    act.wait_ge(slab_done, freed)
                for k in range(4):
                    act.wait_ge(fill_tr, 4 * transposed_before(f) + k + 1)
                    nc.scalar.activation(dst[:, 4 * c + k, :], aux[:, k, 0:P * nt], ACT.Copy).then_inc(fill_hi, 1)

            def fill_y(f, c, freed):
                act.wait_ge(f_loaded[f % 2], 16 * (f // 2 + 1))
                act.wait_ge(slab_done, freed)
                for k in range(4):
                    nc.scalar.activation(act_hi[:, 4 * c + k, :], f_raw[:, f % 2, k, :], ACT.Copy).then_inc(fill_hi, 1)

            def root(n, k=4, at=0):
                act.wait_ge(ms_ready, n)
                nc.scalar.activation(rms[:, at:at + k], ms[:, at:at + k], ACT.Sqrt).then_inc(rms_ready, 1)

            def keys_out(L):
                act.wait_ge(kmt_done, L + 1)
                for n in range(2):
                    last = nc.scalar.activation(km[:, L, 2 * n:2 * n + 2, :],
                                                aux[:, n, :].rearrange("p (a m) -> p a m", a=2), ACT.Copy)
                last.then_inc(kmt_read, 1)

            act.wait_ge(vec_copied, 1)
            for m in range(4):
                for j in range(4):
                    if m == 0:
                        fill(F_MEM + j, j, memt_hi, NMB)
                        split(0, j, g_mem)
                        if j == 3:
                            root(1, NMB)
                            split(1, 0, g_mem)
                            act.wait_ge(lam_in, 1)
                            nc.scalar.activation(lt[:, 1, :], lt[:, 0, :], ACT.Exp).then_inc(lam_exp, 1)
                        continue
                    split_next(m, j, g_mem, g_mem if m < 3 else g_a)
                    if m % 2 == 1 and j == 1:
                        keys_out(m // 2)
                    if j == 2:
                        fill(F_X + m - 1, m - 1, act_hi, NT, 14 if m == 3 else None)

            def mem_scores(L, n):
                act.wait_ge(nmx_ready, 4 * L + n + 1)
                for t in range(NT):
                    last = nc.scalar.activation(pm[:, t, :], aux[:, t // 2, M * (t % 2):M * (t % 2) + M], ACT.Exp,
                                                bias=nmx[:, t:t + 1], scale=SCALE, accum_out=rsum[:, t:t + 1])
                last.then_inc(p_exp, 1)

            def mem_probs_out(L, n):
                act.wait_ge(pt_done, 4 * L + n + 1)
                for m in range(NMB):
                    last = nc.scalar.activation(pmt[:, m, :], aux[:, 2 + m, :], ACT.Copy)
                last.then_inc(pt_read, 1)

            def gate_sigmoid(G, n):
                act.wait_ge(bank_free, 4 * G - 4)
                nc.scalar.activation(block(5), block(4), ACT.Sigmoid).then_inc(sg_ready, 1)

            def store_y(y, i, n):
                act.wait_ge(y_ready, n)
                act.dma_start(y[bass.ds(4 * i, 4)].rearrange("k p t -> p k t"), gg).then_inc(y_stored, 16)

            def mem_branch(L, G, gain, n_y, y, f0):
                for j in range(4):
                    split_next(G, j, gain)
                    if j >= 1:
                        mem_probs_out(L, j - 1)
                    mem_scores(L, j)
                    if j >= 2:
                        fill_y(f0 + j - 2, j - 2, 4 * G + j - 1)
                split_next(G + 1, 0, None)
                mem_probs_out(L, 3)
                gate_sigmoid(G, 0)
                fill_y(f0 + 2, 2, 4 * G + 3)
                store_y(y, 3, n_y)
                split_next(G + 1, 1, None)
                fill_y(f0 + 3, 3, 4 * G + 4)

            for j in range(4):
                split_next(G_A, j, g_a, g_a)
                if j == 1:
                    fill(F_X + 3, 3, act_hi, NT, 16)
                    root(2)
            with act.Fori(0, NPAIR) as i:
                for q in range(2):
                    G = 2 * i + (G_A + 1 + q)
                    for j in range(4):
                        slot = 4 * q + j
                        if slot == 0:
                            for n, w in enumerate((w_rec_gate, w_in_gate)):
                                act.dma_start(gate_w[:, n, :, :], w[0, bass.ds(4 * i, 4)].rearrange("b c d -> c b d")
                                              ).then_inc(gate_loaded, 16)
                        split_next(G, j, g_a, g_a)
                        if slot in (1, 2):
                            for b in (2 * slot - 2, 2 * slot - 1):
                                act.wait_ge(gates_done, 4 * i + b + 1)
                                nc.scalar.activation(ra[:, b, :], aux[:, 2 * (b % 2), :], ACT.Sigmoid,
                                                     bias=chan[:, bass.ds(4 * i + b + 60, 1)])
                                nc.scalar.activation(ig[:, b, :], aux[:, 2 * (b % 2) + 1, :], ACT.Sigmoid,
                                                     bias=chan[:, bass.ds(4 * i + b + 72, 1)]).then_inc(gates_read, 1)
                        if slot == 3:
                            act.wait_ge(gates_read, 4 * i + 4)
                            for b in range(4):
                                nc.scalar.activation(th[:, b, :], ra[:, b, :], ACT.Tanh,
                                                     scale=c_pos[:, bass.ds(4 * i + b, 1)])
                            for b in range(4):
                                nc.scalar.activation(ra[:, b, :], ra[:, b, :], ACT.Exp,
                                                     scale=c_neg[:, bass.ds(4 * i + b, 1)]).then_inc(decay_ready, 1)
                        if slot == 5:
                            act.wait_ge(v_ready, i + 1)
                            nc.scalar.activation(block(3), block(3), ACT.Sqrt).then_inc(root_ready, 1)
                            gate_sigmoid(2 * i + (G_A + 1), 0)
                        if slot == 7:
                            store_y(y_dram, i, i + 1)
            mem_branch(0, G_A + 7, g_a, 4, y_dram, F_YA)

            def load_resid(c):
                act.dma_start(stage, x_v[:, :, bass.ds(C * c, C)]).then_inc(resid_loaded, 16)

            def store_h(c, G):
                act.wait_ge(bank_free, 4 * G - 4)
                act.dma_start(h_v[:, :, bass.ds(C * c, C)], stage).then_inc(h_stored, 16)

            load_resid(0)
            for j in (2, 3):
                split_next(G_OUTA, j, None)
            with act.Fori(0, 2) as i:
                G = i + (G_OUTA + 1)
                for j in range(4):
                    split_next(G, j, None)
                    if j == 0:
                        store_h(i, i + G_OUTA)
                    if j == 1:
                        act.wait_ge(h_stored, 16 * i + 16)
                        load_resid(i + 1)
            for j in range(4):
                split_next(G_OUTA + 3, j, None, g_kv)
                if j == 0:
                    store_h(2, G_OUTA + 2)
                if j == 1:
                    act.wait_ge(h_stored, 48)
                    load_resid(3)
                if j >= 2:
                    fill(F_H + j - 2, j - 2, act_hi, NT, 4 * (G_OUTA + 3) + j - 1)
            for j in range(4):
                if j == 0:
                    split_next(G_KV, j, g_kv)
                    store_h(3, G_OUTA + 3)
                else:
                    split_next(G_KV, j, g_kv, g_kv)
                if j < 2:
                    fill(F_H + 2 + j, 2 + j, act_hi, NT, 4 * (G_OUTA + 3) + j + 3)
                if j == 1:
                    root(3)

            def store_keys(i, G):
                act.wait_ge(bank_free, 4 * G - 4)
                act.dma_start(k_dram[bass.ds(4 * i, 4)].rearrange("h p t -> p h t"), stage).then_inc(kv_stored, 16)

            def store_values(i, G):
                act.wait_ge(bank_free, 4 * G - 4)
                act.dma_start(v_v[:, :, bass.ds(C * i, C)], stage).then_inc(kv_stored, 16)

            with act.Fori(0, 3) as i:
                G = i + (G_KV + 1)
                for j in range(4):
                    split_next(G, j, g_kv, g_kv)
                    if j == 0:
                        store_keys(i, i + G_KV)
            for n in range(2):
                for j in range(4):
                    split_next(G_KV + 4 + n, j, g_kv, g_kv if n == 0 else g_b)
                    if j == 0:
                        store_values(n, G_KV + 3 + n)

            def load_kv(h, r):
                act.dma_start(kbuf[:, r, :], k_dram[bass.ds(h, 1)].rearrange("a p t -> p (a t)")).then_inc(kv_loaded[r], 16)
                act.dma_start(vbuf[:, r, :, :], v_v[:, :, bass.ds(P * h, P)]).then_inc(kv_loaded[r], 16)

            for j in range(4):
                split_next(G_B, j, g_b, g_b)
                if j == 0:
                    store_values(2, G_KV + 5)
                if j == 1:
                    act.wait_ge(kv_stored, 96)
                    load_kv(0, 0)
            with act.Fori(0, NPAIR) as i:
                for q in range(2):
                    G = 2 * i + (G_B + 1 + q)
                    for j in range(4):
                        h, second = (4 * q + j) // 2, j % 2
                        n = 4 * i + h
                        if second:
                            act.wait_ge(wt_done, n + 1)
                            for b, w in enumerate((512, 512, 256)):
                                last = nc.scalar.activation(wt[:, 512 * b:512 * b + w], aux[:, 1 + b, 0:w], ACT.Copy)
                            last.then_inc(wt_read, 1)
                        split_next(G, j, g_b, g_b)
                        if not second:
                            for m, (t, bank, at) in enumerate(Z_ORDER):
                                w = P * (t + 1)
                                z = aux[:, bank, at:at + w]
                                act.wait_ge(z_done, 4 * n + (3 if bank == 2 else m + 1))
                                nc.scalar.activation(keep[:, t, T - w:T], z, ACT.Sigmoid, scale=-SCALE)
                                nc.scalar.activation(beta[:, t, T - w:T], z, ACT.Sigmoid, scale=SCALE).then_inc(z_read, 1)
                            if h < 3:
                                load_kv(n + 1, (h + 1) % 2)
                            else:
                                load_kv((4 * i + 4) % NB, 0)
                        if 4 * q + j == 4:
                            gate_sigmoid(2 * i + (G_B + 1), 0)
                        if 4 * q + j == 7:
                            store_y(y2_dram, i, i + 5)
            act.wait_ge(kv_loaded[0], 32 * 7)
            mem_branch(1, G_B + 7, g_b, 8, y2_dram, F_YB)

            def load_h2(c):
                act.dma_start(h2[:, :, c, :], h_v[:, :, C * c:C * c + C]).then_inc(h2_loaded, 16)

            act.wait_ge(y_stored, 128)
            for c in range(4):
                load_h2(c)
            act.dma_start(fgain, final_norm.rearrange("(a n) -> a n", a=1).broadcast_to([P, D])).then_inc(h2_loaded, 16)
            for j in (2, 3):
                split_next(G_OUTB, j, None)

            def squares(c, t):
                act.wait_ge(bank_free, 4 * (G_OUTB + c) + t - 7)
                if t == 0 and c:
                    act.wait_ge(sq_ready, 4 * c)
                nc.scalar.activation(stage[:, t, :], h2[:, t, c, :], ACT.Square, accum_out=ss[:, t, c:c + 1]
                                     ).then_inc(sq_ready, 1)

            for n in range(1, 4):
                for j in range(4):
                    if not (n == 3 and j == 3):
                        split_next(G_OUTB + n, j, None)
                    if n == 3 and j == 2:
                        nc.scalar.activation(nmx[:], rms[:], ACT.Sqrt)
                    if j == 0:
                        for t in range(NT):
                            squares(n - 1, t)
            for t in range(NT):
                squares(3, t)
                root(4 + t, 1, t)

        @blk.vector
        def _(dve):
            ch = Chain(dve, dve_chain)
            V = nc.vector

            def split(G, j, gain=None):
                for k in range(KS):
                    dve.wait_ge(hi_ready, 4 * (4 * G + j) + k + 1)
                    lo, hi = w_lo[:, j % 2, k, :], w_hi[:, j % 2, k, :].bitcast(F32)
                    if gain is None:
                        ins = V.tensor_tensor(lo, w_raw[:, j % 2, k, :], hi, ALU.subtract)
                    else:
                        ins = V.scalar_tensor_tensor(lo, w_raw[:, j % 2, k, :], gain[:, KS * j + k:KS * j + k + 1], hi,
                                                     ALU.mult, ALU.subtract)
                    ins.then_inc(lo_ready, 1)

            def split_next(G, j, gain, next_gain=None):
                if j < 3:
                    split(G, j + 1, gain)
                else:
                    split(G + 1, 0, next_gain)

            def fill(f, c, hi, lo, nt):
                for k in range(4):
                    dve.wait_ge(fill_hi, 4 * f + k + 1)
                    V.tensor_tensor(lo[:, 4 * c + k, :], aux[:, k, 0:P * nt], hi[:, 4 * c + k, :].bitcast(F32),
                                    ALU.subtract).then_inc(fill_lo, 1)

            def fill_y(f, c):
                for k in range(4):
                    dve.wait_ge(fill_hi, 4 * f + k + 1)
                    V.tensor_tensor(act_lo[:, 4 * c + k, :], f_raw[:, f % 2, k, :],
                                    act_hi[:, 4 * c + k, :].bitcast(F32), ALU.subtract).then_inc(fill_lo, 1)

            def mean_square(k, at=0):
                ch.link(V.reduce_sum(ms[:, at:at + k], ss[:, at:at + k, :], AX_X))
                V.tensor_scalar(ms[:, at:at + k], ms[:, at:at + k], 1.0 / D, EPS, ALU.mult, ALU.add).then_inc(ms_ready, 1)

            def bank(G, b):
                if b == 3:
                    dve.wait_ge(slab_done, 4 * G + 4)
                else:
                    dve.wait_ge(bank_done, 3 * G + b - 7)

            def inverse_root(n, dst, k=4, at=0):
                dve.wait_ge(rms_ready, n)
                r, a = dst[:, at:at + k], rms[:, at:at + k]
                ch.link(V.reciprocal(r, a))
                ch.link(V.tensor_tensor(a, r, r, ALU.mult))
                ch.link(V.tensor_tensor(a, a, ms[:, at:at + k], ALU.mult))
                ch.link(V.tensor_scalar(a, a, -0.5, 1.5, ALU.mult, ALU.add))
                ch.link(V.tensor_tensor(r, r, a, ALU.mult))

            lam = chan[:, 84:96]

            def decay_constants():
                dve.wait_ge(lam_exp, 1)
                ch.link(V.tensor_scalar(lt[:, 2, :], lt[:, 1, :], 2.0, None, ALU.add))
                ch.link(V.reciprocal(lt[:, 3, :], lt[:, 2, :]))
                ch.link(V.tensor_tensor(lt[:, 1, :], lt[:, 1, :], lt[:, 3, :], ALU.mult))
                ch.link(V.tensor_tensor(lt[:, 2, :], lt[:, 1, :], lt[:, 1, :], ALU.mult))
                ch.link(V.tensor_scalar(lt[:, 3, :], lt[:, 2, :], 1.0 / 17, 1.0 / 15, ALU.mult, ALU.add))
                for n in (13, 11, 9, 7, 5, 3, 1):
                    ch.link(V.tensor_tensor(lt[:, 3, :], lt[:, 3, :], lt[:, 2, :], ALU.mult))
                    ch.link(V.tensor_scalar(lt[:, 3, :], lt[:, 3, :], 1.0 / n, None, ALU.add))
                ch.link(V.tensor_tensor(lt[:, 3, :], lt[:, 3, :], lt[:, 1, :], ALU.mult))
                ch.link(V.tensor_scalar(lt[:, 1, :], lam, -1.0, 0.0, ALU.mult, ALU.max))
                ch.link(V.scalar_tensor_tensor(lt[:, 2, :], lt[:, 3, :], 2.0, lt[:, 1, :], ALU.mult, ALU.add))
                V.tensor_scalar(c_neg[:], lt[:, 2, :], -LRU_C, None, ALU.mult).then_inc(lam_ready, 1)
                V.tensor_scalar(c_pos[:], lt[:, 2, :], LRU_C, None, ALU.mult).then_inc(lam_ready, 1)

            def mem_out(m):
                for b in range(NMB):
                    if b == 0:
                        dve.wait_ge(bank_done, m + 1)
                    else:
                        dve.wait_ge(slab_done, 4 * m + 4)
                    dst = stage[:, b, :] if m % 2 == 0 else vm[:, m // 2, b, :]
                    ins = V.tensor_scalar(dst, main[:, 2 * (m % 2) + b, :], rstd_m[:, b:b + 1], None, ALU.mult)
                    ins.then_inc(bank_free, 1)

            dve.wait_ge(vec_t, 1)
            V.tensor_copy(gains[:], main[:, 2, 0:64]).then_inc(vec_copied, 1)
            dve.wait_ge(vec_copied, 1)
            for m in range(4):
                for j in range(4):
                    if m == 0:
                        fill(F_MEM + j, j, memt_hi, memt_lo, NMB)
                        split(0, j, g_mem)
                        if j == 2:
                            dve.wait_ge(vec_t, 2)
                            V.tensor_copy(chan[:], main[:, 3, 0:96]).then_inc(vec_copied, 1)
                            dve.wait_ge(vec_copied, 2)
                            ch.link(V.tensor_scalar(lt[:, 0, :], lam, -1.0, None, ALU.mult))
                            V.tensor_tensor(lt[:, 0, :], lam, lt[:, 0, :], ALU.min).then_inc(lam_in, 1)
                        if j == 3:
                            mean_square(NMB)
                            split(1, 0, g_mem)
                            inverse_root(1, rstd_m, NMB)
                            mem_out(0)
                        continue
                    split_next(m, j, g_mem, g_mem if m < 3 else g_a)
                    if m == 1 and j == 0:
                        decay_constants()
                    if j == 2:
                        fill(F_X + m - 1, m - 1, act_hi, act_lo, NT)
                    if j == 3:
                        mem_out(m)

            def rstd_rows(n):
                inverse_root(n, rstd)
                for t in range(NT):
                    last = V.tensor_scalar(diag[:, t, 0:P], ident[:], rstd[:, t:t + 1], None, ALU.mult)
                last.then_inc(diag_ready, 1)

            def rstd_row_out(n):
                dve.wait_ge(bc_done, n)
                ch.link(V.tensor_copy(rstd_bc[:], aux[:, 3, :]))

            def branch_out(G, b):
                bank(G, b)
                V.tensor_tensor(xr[:, b, 3:3 + T], main[:, b, :], rstd_bc[:], ALU.mult).then_inc(bank_free, 1)

            def gate_out(G, b):
                bank(G, b)
                V.tensor_tensor(gg[:, b, :], main[:, b, :], rstd_bc[:], ALU.mult).then_inc(bank_free, 1)

            def mem_max(L, n):
                dve.wait_ge(ms_done, 4 * L + n + 1)
                ch.link(V.reduce_max(mx[:], aux[:, 0:2, :].rearrange("p a (t m) -> p (a t) m", t=2), AX_X))
                V.tensor_scalar(nmx[:], mx[:], -SCALE, None, ALU.mult).then_inc(nmx_ready, 1)

            def mem_norm_probs(L, n):
                dve.wait_ge(p_exp, 4 * L + n + 1)
                ch.link(V.reciprocal(rinv[:], rsum[:]))
                for t in range(NT):
                    last = V.tensor_scalar(pm[:, t, :], pm[:, t, :], rinv[:, t:t + 1], None, ALU.mult)
                last.then_inc(p_ready, 1)

            def mem_o(L, n):
                dve.wait_ge(mo_done, 4 * L + n + 1)
                V.tensor_copy(ot[:, n, :], aux[:, 2, :]).then_inc(mo_read, 1)

            def mem_branch(L, G, gain, f0):
                for j in range(4):
                    split_next(G, j, gain)
                    mem_max(L, j)
                    if j == 3:
                        dve.wait_ge(y_stored, 64 * L + 48)
                        gate_out(G, 0)
                    mem_norm_probs(L, j)
                    if j == 3:
                        gate_out(G, 1)
                    if j >= 1:
                        mem_o(L, j - 1)
                    if j >= 2:
                        fill_y(f0 + j - 2, j - 2)
                gate_out(G, 2)
                gate_out(G, 3)
                split_next(G + 1, 0, None)
                mem_o(L, 3)
                dve.wait_ge(sg_ready, 4 * L + 4)
                ch.link(V.tensor_tensor(block(4), block(4), block(5), ALU.mult))
                dve.wait_ge(mo_read, 4 * L + 4)
                V.tensor_tensor(block(4), block(4), block(3), ALU.mult).then_inc(y_ready, 1)
                fill_y(f0 + 2, 2)
                split_next(G + 1, 1, None)
                fill_y(f0 + 3, 3)

            for j in range(4):
                split_next(G_A, j, g_a, g_a)
                if j == 1:
                    fill(F_X + 3, 3, act_hi, act_lo, NT)
                    mean_square(4)
                if j == 2:
                    rstd_rows(2)
            rstd_row_out(1)
            for b in range(4):
                branch_out(G_A, b)
            with dve.Fori(0, NPAIR) as i:
                ch.enter(i, 2 * (2 + 2 * (CONV - 2)) + 2 + 6)
                for q in range(2):
                    G = 2 * i + (G_A + 1 + q)
                    for j in range(4):
                        slot = 4 * q + j
                        split_next(G, j, g_a, g_a)
                        if slot in (0, 1):
                            if slot == 0:
                                dve.wait_ge(bank_free, 4 * G - 8)
                            two = (2 * slot, 2 * slot + 1)
                            at = {}
                            for b in two:
                                at[b] = ch.mark(V.tensor_scalar(xc[:, b, :], xr[:, b, 0:T],
                                                                chan[:, bass.ds(4 * i + b, 1)],
                                                                chan[:, bass.ds(4 * i + b + 48, 1)], ALU.mult, ALU.add))
                            for tap in range(1, CONV):
                                for b in two:
                                    ch.wait(at[b])
                                    ins = V.scalar_tensor_tensor(xc[:, b, :], xr[:, b, tap:tap + T],
                                                                 chan[:, bass.ds(4 * i + b + 12 * tap, 1)], xc[:, b, :],
                                                                 ALU.mult, ALU.add)
                                    if tap < CONV - 1:
                                        at[b] = ch.mark(ins)
                                    else:
                                        ins.then_inc(xc_ready, 1)
                        if slot == 3:
                            for b in range(4):
                                gate_out(G, b)
                        if slot == 4:
                            dve.wait_ge(decay_ready, 4 * i + 4)
                            ch.link(V.tensor_tensor(block(5), block(1), block(1), ALU.mult))
                            V.scalar_tensor_tensor(block(3), block(5), 1.0, block(3), ALU.add, ALU.mult).then_inc(v_ready, 1)
                            ch.link(V.tensor_tensor(block(2), block(2), block(0), ALU.mult))
                        if slot == 6:
                            dve.wait_ge(root_ready, i + 1)
                            ch.link(V.tensor_tensor(block(2), block(2), block(3), ALU.mult))
                            for b in range(4):
                                ch.mark(V.tensor_tensor_scan(th[:, b, :], ra[:, b, :], ig[:, b, :], 0.0, ALU.mult, ALU.add))
                            dve.wait_ge(sg_ready, i + 1)
                            ch.link(V.tensor_tensor(block(4), block(4), block(5), ALU.mult))
                            V.tensor_tensor(block(4), block(4), block(3), ALU.mult).then_inc(y_ready, 1)
                        if slot == 7:
                            for b in range(4):
                                branch_out(G, b)
                            dve.wait_ge(y_stored, 16 * i + 16)
                ch.leave(NPAIR)
            mem_branch(0, G_A + 7, g_a, F_YA)

            def h_out(c, G):
                dve.wait_ge(resid_loaded, 16 * c + 16)
                for b in range(4):
                    bank(G, b)
                    V.tensor_tensor(stage[:, b, :], main[:, b, :], stage[:, b, :], ALU.add).then_inc(bank_free, 1)

            for j in (2, 3):
                split_next(G_OUTA, j, None)
            h_out(0, G_OUTA)
            with dve.Fori(0, 2) as i:
                G = i + (G_OUTA + 1)
                for j in range(4):
                    split_next(G, j, None)
                h_out(i + 1, G)
            for j in range(4):
                split_next(G_OUTA + 3, j, None, g_kv)
                if j >= 2:
                    fill(F_H + j - 2, j - 2, act_hi, act_lo, NT)
            h_out(3, G_OUTA + 3)
            for j in range(4):
                split_next(G_KV, j, g_kv, g_kv)
                if j < 2:
                    fill(F_H + 2 + j, 2 + j, act_hi, act_lo, NT)
                if j == 1:
                    mean_square(4)
                    dve.wait_ge(h_stored, 64)
                    rstd_rows(3)
            rstd_row_out(2)

            def keys_out(G):
                for b in range(4):
                    bank(G, b)
                    V.tensor_tensor(stage[:, b, :], main[:, b, :], rstd_bc[:], ALU.mult).then_inc(bank_free, 1)

            def values_out(G):
                for b in range(4):
                    bank(G, b)
                    V.tensor_scalar(stage[:, b, :], main[:, b, :], rstd[:, b:b + 1], None, ALU.mult).then_inc(bank_free, 1)

            keys_out(G_KV)
            with dve.Fori(0, 2) as i:
                G = i + (G_KV + 1)
                for j in range(4):
                    split_next(G, j, g_kv, g_kv)
                dve.wait_ge(kv_stored, 16 * i + 16)
                keys_out(G)
            with dve.Fori(0, 2) as i:
                G = i + (G_KV + 3)
                for j in range(4):
                    split_next(G, j, g_kv, g_kv)
                dve.wait_ge(kv_stored, 16 * i + 48)
                values_out(G)
            for j in range(4):
                split_next(G_KV + 5, j, g_kv, g_b)
            dve.wait_ge(kv_stored, 80)
            values_out(G_KV + 5)

            for j in range(4):
                split_next(G_B, j, g_b, g_b)
                if j == 0:
                    dve.wait_ge(y_ready, 4)
            for b in range(4):
                branch_out(G_B, b)
            PER_B = 4 * 4 * 3 + 1 + 1
            with dve.Fori(0, NPAIR) as i:
                ch.enter(i, PER_B)
                for q in range(2):
                    G = 2 * i + (G_B + 1 + q)
                    for j in range(4):
                        h, second, slot = (4 * q + j) // 2, j % 2, 4 * q + j
                        n = 4 * i + h
                        split_next(G, j, g_b, g_b)
                        if not second:
                            for m, (t, _, _) in enumerate(Z_ORDER):
                                w = P * (t + 1)
                                dve.wait_ge(z_read, 4 * n + m + 1)
                                k, b = keep[:, t, T - w:T], beta[:, t, T - w:T]
                                a1 = ch.mark(V.tensor_tensor(k[:, w - P:w], k[:, w - P:w], m_keep[:], ALU.max))
                                a2 = ch.mark(V.tensor_tensor(b[:, w - P:w], b[:, w - P:w], m_beta[:], ALU.mult))
                                ch.wait(a1)
                                a3 = ch.mark(V.tensor_tensor_scan(k[:, 1:w][:, ::-1], k[:, 1:w][:, ::-1],
                                                                  k[:, 1:w][:, ::-1], 1.0, ALU.mult, ALU.bypass))
                                ch.wait(a3)
                                V.tensor_tensor(b[:, 0:w - 1], b[:, 0:w - 1], k[:, 1:w], ALU.mult).then_inc(w_ready, 1)
                        if slot == 3:
                            dve.wait_ge(y_stored, 16 * i + 64)
                            gate_out(G, 0)
                            gate_out(G, 1)
                        if slot == 5:
                            dve.wait_ge(sg_ready, i + 5)
                            ch.link(V.tensor_tensor(block(4), block(4), block(5), ALU.mult))
                            V.tensor_tensor(gg[:, 0:2, :], gg[:, 0:2, :], ot[:, 0:2, :], ALU.mult)
                        if slot == 7:
                            branch_out(G, 0)
                            branch_out(G, 1)
                        if second:
                            dve.wait_ge(o_done, n + 1)
                            if h < 2:
                                ins = V.tensor_copy(ot[:, h, :], aux[:, 0, :])
                                if h == 1:
                                    ch.mark(ins)
                            elif h == 2:
                                V.tensor_tensor(gg[:, h, :], aux[:, 0, :], gg[:, h, :], ALU.mult)
                            else:
                                V.tensor_tensor(gg[:, h, :], aux[:, 0, :], gg[:, h, :], ALU.mult).then_inc(y_ready, 1)
                        if slot == 3:
                            gate_out(G, 2)
                            gate_out(G, 3)
                        if slot == 7:
                            branch_out(G, 2)
                            branch_out(G, 3)
                ch.leave(NPAIR)
            mem_branch(1, G_B + 7, g_b, F_YB)

            for j in (2, 3):
                split_next(G_OUTB, j, None)
            dve.wait_ge(h2_loaded, 16 * 5)

            def h2_out(c, t):
                bank(G_OUTB + c, t)
                V.tensor_tensor(h2[:, t, c, :], main[:, t, :], h2[:, t, c, :], ALU.add).then_inc(bank_free, 1)

            for t in range(NT):
                h2_out(0, t)
            for c in range(1, 4):
                for j in range(4):
                    if not (c == 3 and j == 3):
                        split_next(G_OUTB + c, j, None)
                    if j == 1:
                        for t in range(NT):
                            dve.wait_ge(sq_ready, 4 * (c - 1) + t + 1)
                            V.tensor_tensor(h2[:, t, c - 1, :], h2[:, t, c - 1, :], fgain[:, C * (c - 1):C * c],
                                            ALU.mult).then_inc(pregain, 1)
                if c < 3:
                    for t in range(NT):
                        h2_out(c, t)
            def scale_tile(t):
                dve.wait_ge(last_gain, t + 1)
                for half in range(2):
                    o = h2[:, t, 2 * half:2 * half + 2, :]
                    V.tensor_scalar(o, o, rstd[:, t:t + 1], rms[:, t:t + 1], ALU.mult, ALU.mult).then_inc(scaled, 1)

            dve.wait_ge(pregain, 12)
            ch.link(V.reduce_sum(mx[:], ss[:, :, 0:3], AX_X))
            ch.link(V.tensor_scalar(mx[:], mx[:], 1.0 / D, EPS, ALU.mult, ALU.add))
            for t in range(NT):
                h2_out(3, t)
                if t:
                    scale_tile(t - 1)
                dve.wait_ge(sq_ready, 12 + t + 1)
                m, r, a = ms[:, t:t + 1], rstd[:, t:t + 1], rms[:, t:t + 1]
                V.tensor_scalar(m, ss[:, t, 3:4], 1.0 / D, mx[:, t:t + 1], ALU.mult, ALU.add).then_inc(ms_ready, 1)
                dve.wait_ge(rms_ready, 4 + t)
                ch.link(V.reciprocal(r, a))
                ch.link(V.scalar_tensor_tensor(a, r, m, r, ALU.mult, ALU.mult))
                ch.link(V.tensor_scalar(a, a, -0.5, 1.5, ALU.mult, ALU.add))
            scale_tile(NT - 1)

        @blk.tensor
        def _(pe):
            TE = nc.tensor

            def slab(G, j, form, hooks=(), wait_banks=True):
                hooks = dict(hooks)
                p = j % 2
                nt = NMB if form == "M" else 4
                for t in range(nt):
                    if t in hooks:
                        hooks[t]()
                    if form == "M":
                        o = main[:, 2 * (G % 2) + t, :]
                        if j == 0 and G >= 2:
                            pe.wait_ge(bank_free, 2 * G + t - 3)
                    else:
                        o = main[:, t, :]
                        if j == 0:
                            pe.wait_ge(bank_free, 4 * G + t - 11)
                    for k in range(KS):
                        kk = KS * j + k
                        if t == 0:
                            pe.wait_ge(lo_ready, 4 * (4 * G + j) + k + 1)
                        wh, wl = w_hi[:, p, k, :], w_lo[:, p, k, :]
                        if form == "M":
                            ah, al = memt_hi[:, kk, P * t:P * t + P], memt_lo[:, kk, P * t:P * t + P]
                            three = ((ah, wh), (ah, wl), (al, wh))
                        elif form == "N":
                            ah, al = act_hi[:, kk, P * t:P * t + P], act_lo[:, kk, P * t:P * t + P]
                            three = ((ah, wh), (ah, wl), (al, wh))
                        else:
                            ah, al = act_hi[:, kk, :], act_lo[:, kk, :]
                            wh, wl = wh[:, P * t:P * t + P], wl[:, P * t:P * t + P]
                            three = ((wh, ah), (wh, al), (wl, ah))
                        for n, (a, b) in enumerate(three):
                            last = TE.matmul(o, a, b, start=kk == 0 and n == 0, stop=kk == NK - 1 and n == 2)
                    if j == 3 and t < nt - 1:
                        last.then_inc(bank_done, 1)
                last.then_inc(slab_done, 1)

            def transpose_fill(f, nt, before=None):
                pe.wait_ge(f_loaded[f % 2], 16 * (f // 2 + 1))
                if before:
                    before()
                for k in range(4):
                    for t in range(nt):
                        last = TE.transpose(aux[:, k, P * t:P * t + P], f_raw[:, f % 2, t, P * k:P * k + P], ident[:])
                    last.then_inc(fill_tr, 1)

            def after_fill(f):
                return lambda: pe.wait_ge(fill_lo, 4 * f + 4)

            def await_fill(f):
                pe.wait_ge(fill_lo, 4 * f + 4)

            pe.wait_ge(const_ready, 3)
            pe.wait_ge(vec_loaded, 16 * 4)
            TE.transpose(main[:, 2, 0:64], vec_raw[0:64, 0, :], ident[0:64, 0:64]).then_inc(vec_t, 1)
            transpose_fill(F_MEM, NMB)

            def chan_transposed():
                pe.wait_ge(chan_loaded, 16 * 5)
                TE.transpose(main[:, 3, 0:96], vec_raw[0:96, 1, :], ident[0:96, 0:96]).then_inc(vec_t, 1)

            def keys_transposed(L):
                pe.wait_ge(bank_free, 4 * L + 2)
                pe.wait_ge(fill_lo, 4 * (F_MEM + 4 if L == 0 else F_X + 2))
                for h in range(MH):
                    for b in range(NMB):
                        last = TE.transpose(aux[:, h // 2, M * (h % 2) + P * b:M * (h % 2) + P * b + P],
                                            stage[:, b, P * h:P * h + P], ident[:])
                last.then_inc(kmt_done, 1)

            for m in range(4):
                if m == 1:
                    pe.wait_ge(vec_copied, 2)
                for j in range(4):
                    hooks = {}
                    if m == 0:
                        await_fill(F_MEM + j)
                        if j < 3:
                            hooks[1] = lambda j=j: transpose_fill(F_MEM + j + 1, NMB, after_fill(F_MEM + j))
                        if j == 2:
                            hooks[0] = chan_transposed
                    if m % 2 == 1 and j == 1:
                        hooks[0] = lambda m=m: keys_transposed(m // 2)
                    if m >= 1 and j == 2:
                        hooks[0] = lambda m=m: transpose_fill(
                            F_X + m - 1, NT, lambda: pe.wait_ge(kmt_read, 1 if m < 3 else 2) if m != 2
                            else pe.wait_ge(fill_lo, 4 * (F_X + 1)))
                    slab(m, j, "M", hooks)

            def rstd_row(n):
                pe.wait_ge(diag_ready, n)
                for t in range(NT):
                    last = TE.matmul(aux[:, 3, P * t:P * t + P], ones[:], diag[:, t, 0:P], start=True, stop=True)
                last.then_inc(bc_done, 1)

            def gates(i, b):
                pe.wait_ge(xc_ready, 4 * i + b + 1)
                if b == 0:
                    pe.wait_ge(gate_loaded, 32 * i + 32)
                if b >= 2:
                    pe.wait_ge(gates_read, 4 * i + b - 1)
                for n in range(2):
                    last = TE.matmul(aux[:, 2 * (b % 2) + n, :], gate_w[:, n, b, :], xc[:, b, :], start=True, stop=True)
                last.then_inc(gates_done, 1)

            def mem_scores(L, n):
                if n == 0:
                    if L == 0:
                        pe.wait_ge(gates_read, 4 * NPAIR)
                    else:
                        pe.wait_ge(y_ready, 4 + NPAIR)
                    pe.wait_ge(bank_free, 4 * ((G_A if L == 0 else G_B) + 6) - 4)
                for t in range(NT):
                    last = TE.matmul(aux[:, t // 2, M * (t % 2):M * (t % 2) + M], xr[:, n, 3 + P * t:3 + P * t + P],
                                     km[:, L, n, :], start=True, stop=True)
                last.then_inc(ms_done, 1)

            def mem_transposed(L, n):
                pe.wait_ge(p_ready, 4 * L + n + 1)
                if n:
                    pe.wait_ge(mo_read, 4 * L + n)
                for m in range(NMB):
                    for t in range(NT):
                        last = TE.transpose(aux[:, 2 + m, P * t:P * t + P], pm[:, t, P * m:P * m + P], ident[:])
                last.then_inc(pt_done, 1)

            def mem_values(L, n):
                pe.wait_ge(pt_read, 4 * L + n + 1)
                for m in range(NMB):
                    last = TE.matmul(aux[:, 2, :], vm[:, L, m, P * n:P * n + P], pmt[:, m, :],
                                     start=m == 0, stop=m == NMB - 1)
                last.then_inc(mo_done, 1)

            def mem_branch(L, G, G_next, f0):
                for j in range(4):
                    hooks = {(1 if j == 0 else 0): lambda: mem_scores(L, j), 3: lambda: mem_transposed(L, j)}
                    if j:
                        hooks[2] = lambda: mem_values(L, j - 1)
                    slab(G, j, "T", hooks)
                for j in range(4):
                    await_fill(f0 + j)
                    slab(G_next, j, "N", {2: lambda: mem_values(L, 3)} if j == 0 else {})

            for j in range(4):
                hooks = {}
                if j == 0:
                    hooks[0] = lambda: await_fill(F_X + 2)
                if j == 1:
                    hooks[0] = lambda: transpose_fill(F_X + 3, NT, after_fill(F_X + 2))
                if j == 3:
                    hooks[0] = lambda: (await_fill(F_X + 3), rstd_row(1))
                slab(G_A, j, "T", hooks)
            with pe.Fori(0, NPAIR) as i:
                for j in range(4):
                    hooks = {}
                    if j in (1, 2):
                        hooks[0] = lambda: (gates(i, 2 * j - 2), gates(i, 2 * j - 1))
                    slab(2 * i + (G_A + 1), j, "T", hooks)
                for j in range(4):
                    slab(2 * i + (G_A + 2), j, "T")
            mem_branch(0, G_A + 7, G_OUTA, F_YA)
            with pe.Fori(0, 2) as i:
                for j in range(4):
                    slab(i + (G_OUTA + 1), j, "N")
            for j in range(4):
                hooks = {}
                if j == 2:
                    hooks[0] = lambda: transpose_fill(F_H, NT, lambda: pe.wait_ge(mo_read, 4))
                if j == 3:
                    hooks[0] = lambda: transpose_fill(F_H + 1, NT, after_fill(F_H))
                slab(G_OUTA + 3, j, "N", hooks)
            for j in range(4):
                if j < 2:
                    hooks = {0: lambda: transpose_fill(F_H + 2 + j, NT, after_fill(F_H + 1 + j))}
                elif j == 2:
                    hooks = {}
                else:
                    hooks = {0: lambda: (await_fill(F_H + 3), rstd_row(2))}
                if j == 0:
                    await_fill(F_H)
                if j == 2:
                    await_fill(F_H + 2)
                slab(G_KV, j, "T", hooks)
            with pe.Fori(0, 2) as i:
                for j in range(4):
                    slab(i + (G_KV + 1), j, "T")
            with pe.Fori(0, 3) as i:
                for j in range(4):
                    slab(i + (G_KV + 3), j, "N")

            def stick_scores(i, h):
                n = 4 * i + h
                pe.wait_ge(kv_loaded[h % 2], 32 * (2 * i + h // 2 + 1))
                if h == 0:
                    pe.wait_ge(bank_free, 4 * (2 * i + G_B) - 4)
                for t, bank, at in Z_ORDER:
                    w = P * (t + 1)
                    TE.matmul(aux[:, bank, at:at + w], xr[:, h, 3 + P * t:3 + P * t + P], kbuf[:, h % 2, 0:w],
                              start=True, stop=True).then_inc(z_done, 1)

            def stick_transposed(i, h):
                pe.wait_ge(w_ready, 4 * (4 * i + h) + 4)
                for k in range(NT):
                    bank, at = ((1, 0), (2, 0), (3, 0), (2, 384))[k]
                    for t in range(k, NT):
                        o = aux[:, bank, at + P * (t - k):at + P * (t - k) + P]
                        c = T - P * (t + 1) + P * k
                        last = TE.transpose(o, beta[:, t, c:c + P], ident[:])
                last.then_inc(wt_done, 1)

            def stick_values(i, h):
                pe.wait_ge(wt_read, 4 * i + h + 1)
                for k in range(NT):
                    at = (0, 512, 1024, 896)[k]
                    last = TE.matmul(aux[:, 0, P * k:T], vbuf[:, h % 2, k, :], wt[:, at:at + T - P * k],
                                     start=k == 0, stop=k == NT - 1)
                last.then_inc(o_done, 1)

            for j in range(4):
                slab(G_B, j, "T")
            with pe.Fori(0, NPAIR) as i:
                for q in range(2):
                    for j in range(4):
                        h = 2 * q + j // 2
                        if j % 2 == 0:
                            hooks = {(1 if h == 0 else 0): lambda: stick_scores(i, h)}
                        else:
                            hooks = {0: lambda: stick_transposed(i, h), 2: lambda: stick_values(i, h)}
                        slab(2 * i + (G_B + 1 + q), j, "T", hooks)
            mem_branch(1, G_B + 7, G_OUTB, F_YB)
            with pe.Fori(0, 3) as i:
                for j in range(4):
                    slab(i + (G_OUTB + 1), j, "N")


_INS = ["x", "mem", "mem_norm", "w_mem_kv", "norm_a", "w_in_a", "conv_w", "conv_b", "w_rec_gate", "b_rec_gate",
        "w_in_gate", "b_in_gate", "lru_lambda", "w_out_a", "kv_norm", "w_kv", "norm_b", "w_in_b", "w_out_b",
        "final_norm"]


def kernel(**inputs):
    import concourse.bacc as bacc
    import numpy as np
    from concourse.bass_utils import run_bass_kernel_spmd

    nc = bacc.Bacc("TRN2", target_bir_lowering=False, num_devices=1, dynamic_dma_scratch_size=1024)
    arrays, args = {}, []
    for name in _INS:
        a = np.ascontiguousarray(inputs[name])
        arrays[f"in_{name}"] = a
        args.append(nc.dram_tensor(f"in_{name}", a.shape, mybir.dt.from_np(a.dtype), kind="ExternalInput").ap())
    args.append(nc.dram_tensor("out", (1, T, D), F32, kind="ExternalOutput").ap())
    trunk(nc, *args)
    r = run_bass_kernel_spmd(nc, [arrays], core_ids=[0])
    return r.results[0]["out"]
```
